# Optimizing a Trainium2 kernel written in Bass

```python
import math
import jax, jax.numpy as jnp
from jax import lax
import numpy as np

D_MODEL = 1024
BATCH = 1
SEQ = 256
DEPTH = 1

HEAD_DIM = D_MODEL // 8
DN_HEADS = 4
DN_DK = HEAD_DIM
DN_DV = HEAD_DIM
DN_CONV = 4
DN_CHUNK = 64
FOX_HEADS = 4
FOX_HD = HEAD_DIM
FOX_BLOCK = 128
MOE_EXPERTS = 32
MOE_TOPK = 4
MOE_FF = D_MODEL
MOE_BLOCK = 128
SWIGLU_LIMIT = 7.0
SWIGLU_ALPHA = 1.702
N_MOD = 6
RMS_EPS = 1e-6
L2_EPS = 1e-6

DN_QKV = DN_HEADS * (2 * DN_DK + DN_DV)
DN_W = DN_HEADS * DN_DV
FOX_W = FOX_HEADS * FOX_HD
IN_SIZES = (DN_QKV, DN_W, DN_HEADS, DN_HEADS, 3 * FOX_W, FOX_HEADS, D_MODEL, D_MODEL)
N_IN = sum(IN_SIZES)

kernel_name = "hybrid_deltanet_fox_moe_adaln"

def rms_norm(x, g):
    xf = x.astype(jnp.float32)
    y = xf * lax.rsqrt(jnp.mean(xf * xf, axis=-1, keepdims=True) + RMS_EPS)
    return (y * g.astype(jnp.float32)).astype(x.dtype)

def l2_normalize(x):
    return x * lax.rsqrt(jnp.sum(x * x, axis=-1, keepdims=True) + L2_EPS)

def causal_depthwise_conv(x, w):
    K, C = w.shape
    return lax.conv_general_dilated(x, w[:, None, :].astype(x.dtype), window_strides=(1,),
                                    padding=[(K - 1, 0)], dimension_numbers=("NWC", "WIO", "NWC"),
                                    feature_group_count=C)

def gated_delta_rule(q, k, v, g, beta):
    B, S, H, DK = q.shape
    DV = v.shape[-1]
    C = DN_CHUNK
    N = S // C
    f32 = jnp.float32
    q = l2_normalize(q.astype(f32)) * (DK ** -0.5)
    k = l2_normalize(k.astype(f32))
    v = v.astype(f32)

    def chunks(t):
        return jnp.transpose(t.reshape(B, N, C, H, t.shape[-1]), (0, 3, 1, 2, 4))

    q, k, v = chunks(q), chunks(k), chunks(v)
    g = jnp.transpose(g.astype(f32).reshape(B, N, C, H), (0, 3, 1, 2))
    beta = jnp.transpose(beta.astype(f32).reshape(B, N, C, H), (0, 3, 1, 2))
    gc = jnp.cumsum(g, axis=-1)
    incl = jnp.tril(jnp.ones((C, C), dtype=bool))
    strict = jnp.tril(jnp.ones((C, C), dtype=bool), -1)
    decay = jnp.exp(jnp.where(incl, gc[..., :, None] - gc[..., None, :], -jnp.inf))
    kb = k * beta[..., None]
    vb = v * beta[..., None]
    L = jnp.where(strict, jnp.einsum("bhncd,bhnmd->bhncm", kb, k) * decay, 0.0)
    eye = jnp.eye(C, dtype=f32)
    T = lax.linalg.triangular_solve(L + eye, jnp.broadcast_to(eye, L.shape), left_side=True, lower=True)
    u = jnp.einsum("bhncm,bhnmv->bhncv", T, vb)
    w = jnp.einsum("bhncm,bhnmk->bhnck", T, kb * jnp.exp(gc)[..., None])
    attn = jnp.where(incl, jnp.einsum("bhncd,bhnmd->bhncm", q, k) * decay, 0.0)
    q_dec = q * jnp.exp(gc)[..., None]
    g_last = gc[..., -1]
    k_dec = k * jnp.exp(g_last[..., None] - gc)[..., None]
    xs = tuple(jnp.moveaxis(t, 2, 0) for t in (u, w, q_dec, k_dec, attn, g_last))

    def step(state, inp):
        u_n, w_n, qd_n, kd_n, a_n, gl_n = inp
        v_new = u_n - jnp.einsum("bhck,bhkv->bhcv", w_n, state)
        o = jnp.einsum("bhck,bhkv->bhcv", qd_n, state) + jnp.einsum("bhcm,bhmv->bhcv", a_n, v_new)
        state = state * jnp.exp(gl_n)[..., None, None] + jnp.einsum("bhck,bhcv->bhkv", kd_n, v_new)
        return state, o

    state0 = jnp.zeros((B, H, DK, DV), f32)
    _, o = lax.scan(step, state0, xs)
    return jnp.transpose(o, (1, 0, 3, 2, 4)).reshape(B, S, H, DV)

def forgetting_attention(q, k, v, log_f):
    B, S, H, Dh = q.shape
    nb = S // FOX_BLOCK
    scale = Dh ** -0.5
    F = jnp.cumsum(log_f.astype(jnp.float32), axis=1)
    F_k = jnp.transpose(F, (0, 2, 1))
    q_blocks = jnp.moveaxis(q.reshape(B, nb, FOX_BLOCK, H, Dh), 1, 0)
    F_blocks = jnp.moveaxis(F.reshape(B, nb, FOX_BLOCK, H), 1, 0)
    k_pos = jnp.arange(S)

    def block(args):
        q_blk, F_blk, b_idx = args
        s = jnp.einsum("bqhd,bkhd->bhqk", q_blk, k).astype(jnp.float32) * scale
        s = s + jnp.transpose(F_blk, (0, 2, 1))[..., None] - F_k[:, :, None, :]
        q_pos = b_idx * FOX_BLOCK + jnp.arange(FOX_BLOCK)
        s = jnp.where(k_pos[None, :] <= q_pos[:, None], s, -jnp.inf)
        p = jax.nn.softmax(s, axis=-1).astype(v.dtype)
        return jnp.einsum("bhqk,bkhd->bqhd", p, v)

    o = lax.map(block, (q_blocks, F_blocks, jnp.arange(nb)))
    return jnp.moveaxis(o, 0, 1).reshape(B, S, H, Dh)

def moe_ffn(h, w_router, b_router, w_gate_up, b_gate_up, w_down, b_down):
    B, S, D = h.shape
    T = B * S
    A = T * MOE_TOPK
    xt = h.reshape(T, D)
    logits = (xt @ w_router + b_router).astype(jnp.float32)
    top_val, top_idx = lax.top_k(logits, MOE_TOPK)
    gates = jax.nn.softmax(top_val, axis=-1)
    e_flat = top_idx.reshape(A).astype(jnp.int32)
    tok_flat = jnp.arange(A, dtype=jnp.int32) // MOE_TOPK
    g_flat = gates.reshape(A)
    order = jnp.argsort(e_flat)
    e_sorted = e_flat[order]
    counts = jnp.bincount(e_flat, length=MOE_EXPERTS).astype(jnp.int32)
    padded = (counts + MOE_BLOCK - 1) // MOE_BLOCK * MOE_BLOCK
    pad_end = jnp.cumsum(padded)
    pad_start = pad_end - padded
    grp_start = jnp.cumsum(counts) - counts
    dest = pad_start[e_sorted] + (jnp.arange(A, dtype=jnp.int32) - grp_start[e_sorted])
    n_blocks = -(-A // MOE_BLOCK) + MOE_EXPERTS
    P = n_blocks * MOE_BLOCK
    tok_buf = jnp.full((P,), T, jnp.int32).at[dest].set(tok_flat[order])
    gate_buf = jnp.zeros((P,), jnp.float32).at[dest].set(g_flat[order])
    blk_start = jnp.arange(n_blocks, dtype=jnp.int32) * MOE_BLOCK
    blk_e = jnp.minimum(jnp.searchsorted(pad_end, blk_start, side="right"), MOE_EXPERTS - 1)
    x_pad = jnp.concatenate([xt, jnp.zeros((1, D), xt.dtype)], axis=0)
    x_buf = x_pad[tok_buf].reshape(n_blocks, MOE_BLOCK, D)

    def expert_block(args):
        xb, e = args
        gu = xb @ w_gate_up[e] + b_gate_up[e]
        gate, up = gu[:, :MOE_FF], gu[:, MOE_FF:]
        gate = jnp.minimum(gate, SWIGLU_LIMIT)
        up = jnp.clip(up, -SWIGLU_LIMIT, SWIGLU_LIMIT)
        act = (up + 1.0) * (gate * jax.nn.sigmoid(SWIGLU_ALPHA * gate))
        return act @ w_down[e] + b_down[e]

    y_buf = lax.map(expert_block, (x_buf, blk_e)).reshape(P, D)
    y = jnp.zeros((T + 1, D), jnp.float32).at[tok_buf].add(y_buf.astype(jnp.float32) * gate_buf[:, None])
    return y[:T].reshape(B, S, D).astype(h.dtype)

def setup_inputs(seed: int = 0) -> dict:
    key = jax.random.key(seed)
    ks = jax.random.split(key, 24)
    f32 = jnp.float32
    nrm = jax.random.normal
    x = nrm(ks[0], (BATCH, SEQ, D_MODEL), f32)
    c = nrm(ks[1], (BATCH, D_MODEL), f32)
    w_ada = nrm(ks[2], (DEPTH, D_MODEL, N_MOD * D_MODEL), f32) * (0.5 * D_MODEL ** -0.5)
    b_ada = 0.02 * nrm(ks[3], (DEPTH, N_MOD * D_MODEL), f32)
    g_norm1 = 1.0 + 0.02 * nrm(ks[4], (DEPTH, D_MODEL), f32)
    w_in = nrm(ks[5], (DEPTH, D_MODEL, N_IN), f32) * D_MODEL ** -0.5
    conv_w = nrm(ks[6], (DEPTH, DN_CONV, DN_QKV), f32) * DN_CONV ** -0.5
    a_log = jnp.log(jax.random.uniform(ks[7], (DEPTH, DN_HEADS), f32, 1.0, 16.0))
    dt = jnp.exp(jax.random.uniform(ks[8], (DEPTH, DN_HEADS), f32, math.log(1e-3), math.log(1e-1)))
    dt_bias = jnp.log(jnp.expm1(dt))
    g_onorm = 1.0 + 0.02 * nrm(ks[9], (DEPTH, DN_DV), f32)
    b_fgate = jax.random.uniform(ks[10], (DEPTH, FOX_HEADS), f32, 1.0, 4.0)
    w_o_delta = nrm(ks[11], (DEPTH, DN_W, D_MODEL), f32) * DN_W ** -0.5
    w_o_fox = nrm(ks[12], (DEPTH, FOX_W, D_MODEL), f32) * FOX_W ** -0.5
    w_out = nrm(ks[13], (DEPTH, D_MODEL, D_MODEL), f32) * D_MODEL ** -0.5
    g_norm2 = 1.0 + 0.02 * nrm(ks[14], (DEPTH, D_MODEL), f32)
    w_router = nrm(ks[15], (DEPTH, D_MODEL, MOE_EXPERTS), f32) * D_MODEL ** -0.5
    b_router = 0.01 * nrm(ks[16], (DEPTH, MOE_EXPERTS), f32)
    w_gate_up = nrm(ks[17], (DEPTH, MOE_EXPERTS, D_MODEL, 2 * MOE_FF), f32) * D_MODEL ** -0.5
    b_gate_up = 0.01 * nrm(ks[18], (DEPTH, MOE_EXPERTS, 2 * MOE_FF), f32)
    w_down = nrm(ks[19], (DEPTH, MOE_EXPERTS, MOE_FF, D_MODEL), f32) * MOE_FF ** -0.5
    b_down = 0.01 * nrm(ks[20], (DEPTH, MOE_EXPERTS, D_MODEL), f32)
    g_final = 1.0 + 0.02 * nrm(ks[21], (D_MODEL,), f32)
    return {"x": x, "c": c, "w_ada": w_ada, "b_ada": b_ada, "g_norm1": g_norm1, "w_in": w_in,
            "conv_w": conv_w, "a_log": a_log, "dt_bias": dt_bias, "g_onorm": g_onorm, "b_fgate": b_fgate,
            "w_o_delta": w_o_delta, "w_o_fox": w_o_fox, "w_out": w_out, "g_norm2": g_norm2,
            "w_router": w_router, "b_router": b_router, "w_gate_up": w_gate_up, "b_gate_up": b_gate_up,
            "w_down": w_down, "b_down": b_down, "g_final": g_final}

def reference(x, c, w_ada, b_ada, g_norm1, w_in, conv_w, a_log, dt_bias, g_onorm, b_fgate,
              w_o_delta, w_o_fox, w_out, g_norm2, w_router, b_router, w_gate_up, b_gate_up,
              w_down, b_down, g_final):
    B, S, D = x.shape
    split_points = np.cumsum(IN_SIZES)[:-1].tolist()
    for l in range(DEPTH):
        mod = (c @ w_ada[l] + b_ada[l]).reshape(B, N_MOD, D)
        sh1, sc1, gt1, sh2, sc2, gt2 = [mod[:, i, None, :] for i in range(N_MOD)]

        h = rms_norm(x, g_norm1[l]) * (1.0 + sc1) + sh1
        proj = h @ w_in[l]
        dn_qkv, dn_z, dn_b, dn_a, fx_qkv, fx_f, gate_a, gate_b = jnp.split(proj, split_points, axis=-1)

        qkv = jax.nn.silu(causal_depthwise_conv(dn_qkv, conv_w[l]))
        q_a, k_a, v_a = jnp.split(qkv, [DN_HEADS * DN_DK, 2 * DN_HEADS * DN_DK], axis=-1)
        q_a = q_a.reshape(B, S, DN_HEADS, DN_DK)
        k_a = k_a.reshape(B, S, DN_HEADS, DN_DK)
        v_a = v_a.reshape(B, S, DN_HEADS, DN_DV)
        beta = jax.nn.sigmoid(dn_b.astype(jnp.float32))
        g = -jnp.exp(a_log[l]) * jax.nn.softplus(dn_a.astype(jnp.float32) + dt_bias[l])
        o_a = gated_delta_rule(q_a, k_a, v_a, g, beta).astype(x.dtype)
        o_a = rms_norm(o_a, g_onorm[l]) * jax.nn.silu(dn_z.reshape(B, S, DN_HEADS, DN_DV))
        y_a = o_a.reshape(B, S, DN_W) @ w_o_delta[l]

        q_b, k_b, v_b = jnp.split(fx_qkv, [FOX_W, 2 * FOX_W], axis=-1)
        log_f = jax.nn.log_sigmoid(fx_f.astype(jnp.float32) + b_fgate[l])
        o_b = forgetting_attention(q_b.reshape(B, S, FOX_HEADS, FOX_HD), k_b.reshape(B, S, FOX_HEADS, FOX_HD),
                                   v_b.reshape(B, S, FOX_HEADS, FOX_HD), log_f)
        y_b = o_b.reshape(B, S, FOX_W) @ w_o_fox[l]

        merged = jax.nn.sigmoid(gate_a) * y_a + jax.nn.sigmoid(gate_b) * y_b
        x = x + gt1 * (merged @ w_out[l])

        h2 = rms_norm(x, g_norm2[l]) * (1.0 + sc2) + sh2
        x = x + gt2 * moe_ffn(h2, w_router[l], b_router[l], w_gate_up[l], b_gate_up[l], w_down[l], b_down[l])
    return rms_norm(x, g_final)


_drawn_inputs = setup_inputs


def setup_inputs(seed=0):
    import zlib

    import numpy as np

    out = dict(_drawn_inputs(seed))
    spreads = {}
    factors = {'g_norm1': 2.874,
     'g_onorm': 4.882,
     'b_gate_up': 55.644,
     'b_down': 64.0,
     'g_final': 7.412,
     'g_norm2': 6.842,
     'b_router': 7.585}
    for name, (base, spread) in spreads.items():
        noise = np.random.default_rng([zlib.crc32(name.encode()), seed]).standard_normal(out[name].shape)
        drawn = base * np.exp(spread * noise) if base else spread * noise
        out[name] = __import__('jax').numpy.asarray(drawn.astype(out[name].dtype))
    for name, factor in factors.items():
        out[name] = (out[name] * factor).astype(out[name].dtype)
    return out
```

```python
from contextlib import ExitStack

import concourse.bass as bass
from concourse import mybir

F32 = mybir.dt.float32
U32 = mybir.dt.uint32
ALU = mybir.AluOpType
ACT = mybir.ActivationFunctionType
AX = mybir.AxisListType

P = 128
BIG = 1e30


def mask_columns():
    kept = [("ident", P), ("iota_slot", 64), ("iota_expert", 32), ("rms_eps", 1), ("ones", P), ("before", P)]
    early = [("cum_chunk", P), ("suffix_chunk", P), ("cum_all_ones", 2 * P),
             ("outside_strict", P), ("outside_incl_t", P), ("fox_open", P), ("fox_outside", P)]
    early += [(f"level{s}", P) for s in range(6)]
    out = []
    for pack in (kept, early):
        at, d = 0, {}
        for name, w in pack:
            d[name] = (at, w)
            at += w
        out.append((d, at))
    return out


def layer_kernel(nc, x, c, w_ada, b_ada, g_norm1, w_in, conv_w, a_log, dt_bias, g_onorm, b_fgate,
                 w_o_delta, w_o_fox, w_out, g_norm2, w_router, b_router, w_gate_up, b_gate_up,
                 w_down, b_down, g_final, kept_masks, early_masks, out):
    T, D = x.shape[1], x.shape[2]
    KD = D // P
    TT = T // P
    HD = g_onorm.shape[1]
    H = a_log.shape[1]
    CH = 64
    NCH = T // CH
    E = w_router.shape[2]
    FF = w_down.shape[2]
    SLOTS = 64
    PAIRS = E // 2
    TOPK = 4
    SCALE = float(HD) ** -0.5
    LIMIT, ALPHA = 7.0, 1.702
    EPS = 1e-6
    UNIT = 2048
    NSTREAM = 8
    LEVELS = 6
    QKV = 3 * H * HD
    W = H * HD
    COL_Z = QKV
    COL_SMALL = COL_Z + W
    COL_FOX = COL_SMALL + 2 * H
    COL_F = COL_FOX + 3 * W
    COL_GATES = COL_F + H
    (KEPT, NKEPT), (EARLY, NEARLY) = mask_columns()

    with ExitStack() as ctx:
        ring = ctx.enter_context(nc.sbuf_tensor("ring", [P, 20, UNIT], F32))
        PERSIST = 12170
        kept = ctx.enter_context(nc.sbuf_tensor("kept", [P, PERSIST], F32))
        ps = ctx.enter_context(nc.psum_tensor("ps", [P, 8, 512], F32))

        sems = {}

        def S(name):
            if name not in sems:
                sems[name] = ctx.enter_context(nc.semaphore(name))
            return sems[name]

        flat = ring[:, :, :].rearrange("p u n -> p (u n)")

        def arena(at, n):
            return flat[:, NSTREAM * UNIT + at:NSTREAM * UNIT + at + n]

        def keep(at, n):
            return kept[:, at:at + n]

        h2tok = keep(0, 2048).rearrange("p (t d) -> p t d", t=TT)
        bias_gu = keep(4096, 512)
        sel = keep(4608, 512).rearrange("p (e q c) -> p e q c", e=2, q=4)
        xg = keep(5120, 1024).rearrange("p (k c) -> p k c", k=KD)
        ypair = keep(6144, 1024)
        gate_a = keep(7168, 512)
        up_a = keep(7680, 512)
        sig_a = act_t = keep(8192, 512)
        onehot = keep(8704, 256).rearrange("p (t c) -> p t c", t=TT)
        gated = keep(8960, 256).rearrange("p (t c) -> p t c", t=TT)
        scat = keep(9216, 256)
        masks_kept = keep(9472, NKEPT)
        o = 9472 + NKEPT
        posm = keep(o, 64).rearrange("p (t e) -> p t e", t=TT)
        gate_w = keep(o + 64, 64).rearrange("p (t e) -> p t e", t=TT)
        mod = keep(o + 128, 48)
        vecs = keep(o + 176, 121)
        small = keep(o + 297, 640)
        wrout = keep(o + 937, 256).rearrange("p (k c) -> p k c", k=KD)
        gt2_row = keep(o + 1193, 1024)
        assert o + 1193 + 1024 <= PERSIST

        xtok = keep(0, 2048).rearrange("p (t d) -> p t d", t=TT)
        xT = keep(6144, 2048).rearrange("p (k n) -> p k n", k=KD)
        hT = keep(4096, 2048).rearrange("p (k n) -> p k n", k=KD)
        merged = keep(4096, 2048).rearrange("p (k n) -> p k n", k=KD)
        gt2b = keep(0, 1024).rearrange("p (k n) -> p k n", k=KD)
        rs2 = keep(1024, 256)
        x1sq = keep(2048, 2048).rearrange("p (k n) -> p k n", k=KD)
        mod_rows = keep(8704, 512)
        small_t = keep(9216, 256)
        fox_p0 = keep(0, 512).rearrange("p (h n) -> p h n", h=H)
        fox_p1 = keep(512, 1024).rearrange("p (h n) -> p h n", h=H)
        fox_e0 = keep(2048, 512).rearrange("p (h n) -> p h n", h=H)
        fox_e1 = keep(2560, 1024).rearrange("p (h n) -> p h n", h=H)
        fox_pt0 = keep(2048, 1024).rearrange("p (h n) -> p h n", h=H)
        fox_pt1 = keep(3072, 512).rearrange("p (h n) -> p h n", h=H)

        gates = arena(0, 4096).rearrange("p (m n) -> p m n", n=T)
        zT = arena(4096, 1024).rearrange("p (m n) -> p m n", n=T)
        RAW = T + 3
        raw = arena(5120, 12 * RAW).rearrange("p (m n) -> p m n", n=RAW)
        qkv = arena(8228, 3072).rearrange("p (m n) -> p m n", n=T)
        qn, kn, vT = qkv[:, 0:4, :], qkv[:, 4:8, :], qkv[:, 8:12, :]
        fqk = arena(11300, 2048).rearrange("p (m n) -> p m n", n=T)
        fv = arena(13348, 1024).rearrange("p (t n) -> p t n", t=TT)
        masks_early = arena(14372, NEARLY)
        gb = arena(16292, 2048).rearrange("p (t h n) -> p t h n", t=TT, h=2 * H)
        kbx = arena(18340, 1024).rearrange("p (t h n) -> p t h n", t=TT, h=H)
        vb = arena(19364, 1024).rearrange("p (t h n) -> p t h n", t=TT, h=H)
        kd = arena(20388, 1024).rearrange("p (t h n) -> p t h n", t=TT, h=H)
        attn_t = arena(21412, 1024).rearrange("p (t h n) -> p t h n", t=TT, h=H)
        tmp = arena(22436, 2048)
        Lm = arena(5120, 1024).rearrange("p (t h n) -> p t h n", t=TT, h=H)
        Mm = arena(6144, 1024).rearrange("p (t h n) -> p t h n", t=TT, h=H)
        Rm = arena(7168, 1024).rearrange("p (t h n) -> p t h n", t=TT, h=H)
        Xm = arena(16292, 1024).rearrange("p (t h n) -> p t h n", t=TT, h=H)
        Um = arena(17316, 1024).rearrange("p (t h n) -> p t h n", t=TT, h=H)
        dec_l = arena(22436, 1024).rearrange("p (t h n) -> p t h n", t=TT, h=H)
        dec_a = arena(23460, 1024).rearrange("p (t h n) -> p t h n", t=TT, h=H)
        u_sb = dec_l
        w_t = dec_a
        state = Lm[:, 0]
        vnew = Mm
        o_sb = Rm
        exg = keep(o + 1193, 1024).rearrange("p (h n) -> p h n", h=H)
        oaT = arena(12324, 1024).rearrange("p (h n) -> p h n", h=H)
        obT = arena(11300, 1024).rearrange("p (h n) -> p h n", h=H)

        def km(name):
            a, w = KEPT[name]
            return masks_kept[:, a:a + w]

        def em(name, w=None):
            a, w0 = EARLY[name]
            return masks_early[:, a:a + (w or w0)]

        ident = km("ident")
        _at = [0]

        def sm(n):
            _at[0] += n
            assert _at[0] <= 640
            return small[:, _at[0] - n:_at[0]]

        s12 = sm(24).rearrange("p (t c) -> p t c", t=TT)
        alog_b, dt_b, fg_b = sm(4), sm(4), sm(4)
        beta = sm(8).rearrange("p (t h) -> p t h", t=TT)
        y8, ab8, e8, u8, l8, g8 = [sm(16).rearrange("p (t h) -> p t h", t=TT) for _ in range(6)]
        ea = sm(4)
        cums = sm(48).rearrange("p (a t h) -> p a t h", a=3, t=TT)
        bx = sm(8).rearrange("p (t h) -> p t h", t=TT)
        kdf = sm(8).rearrange("p (t h) -> p t h", t=TT)
        eg = sm(16).rearrange("p (h n) -> p h n", h=H)
        A1, A2 = sm(8), sm(8)
        fmax, fsum = sm(8).rearrange("p (t h) -> p t h", t=TT), sm(8).rearrange("p (t h) -> p t h", t=TT)
        oss = sm(8).rearrange("p (t h) -> p t h", t=TT)
        brout = sm(32)
        top8 = sm(16).rearrange("p (t j) -> p t j", t=TT)
        idx8 = sm(16).rearrange("p (t j) -> p t j", t=TT)
        ssum = sm(4)
        rounds_f, rounds_part = sm(1), sm(1)
        counts = sm(32)
        lg, part, chosen = [sm(64).rearrange("p (t e) -> p t e", t=TT) for _ in range(3)]
        idx_u = sm(16).bitcast(U32).rearrange("p (t j) -> p t j", t=TT)
        rounds_u = sm(1).bitcast(U32)
        cb = keep(8192, 256).rearrange("p (k c) -> p k c", k=KD)
        wsmall = arena(21412, KD * 12).rearrange("p (k c) -> p k c", k=KD)
        rstd = gt2_row[:, 0:256]
        BCVEC = {"c": 0, "b_ada": KD, "g1": 7 * KD, "g2": 8 * KD, "conv": 9 * KD, "go": 9 * KD + 48}
        vrows = tmp[:, 0:P]
        x2 = flat[:, 2048:4096].rearrange("p (t d) -> p t d", t=TT)
        x2sq = flat[:, 4096:6144].rearrange("p (t d) -> p t d", t=TT)

        def vec(name, i=0, n=1):
            return vecs[:, BCVEC[name] + i:BCVEC[name] + i + n]

        def extra_rounds(eng, one_round):
            eng.wait_ge(S("rounds_ready"), 1)
            n = eng.value_load(rounds_u[0:1, 0:1], min_val=0, max_val=T // SLOTS - 1)
            with eng.If(n > 0):
                with eng.Fori(1, n + 1) as q:
                    one_round(q)
            return n

        def wait_past_first(eng, sem, count):
            if not (isinstance(count, int) and count == 0):
                eng.wait_ge(sem, count)

        def bank(b, a=0, n=512):
            return ps[:, b, a:a + n]

        win3 = w_in[0].rearrange("(k p) n -> p k n", p=P)

        def ada_unit(part, k):
            return w_ada[0, k * P:(k + 1) * P, part * UNIT:(part + 1) * UNIT], None

        def win_unit(col):
            return win3[:, :, col:col + 256], ("p (k n) -> p k n", dict(k=KD))

        def rows_unit(w, r0, kk):
            return (w[0, r0:r0 + kk * P, :].rearrange("(k p) n -> p k n", p=P), ("p (k n) -> p k n", dict(k=kk)))

        UNITS = [("ada0", k, ada_unit(0, k)) for k in range(KD)]
        UNITS += [("dn", u, win_unit(256 * u)) for u in range(6)]
        UNITS += [("fqk", u, win_unit(COL_FOX + 256 * u)) for u in range(4)]
        UNITS += [("fv", u, win_unit(COL_FOX + 2 * W + 256 * u)) for u in range(2)]
        UNITS += [("z", u, win_unit(COL_Z + 256 * u)) for u in range(2)]
        UNITS += [("ada1", k, ada_unit(1, k)) for k in range(KD)]
        UNITS += [("gates", u, win_unit(COL_GATES + 256 * u)) for u in range(8)]
        UNITS += [("ada2", k, ada_unit(2, k)) for k in range(KD)]
        UNITS += [("wo_delta", u, rows_unit(w_o_delta, 256 * u, 2)) for u in range(2)]
        UNITS += [("wo_fox", u, rows_unit(w_o_fox, 256 * u, 2)) for u in range(2)]
        UNITS += [("w_out", u, rows_unit(w_out, 256 * u, 2)) for u in range(4)]
        NUNITS = len(UNITS)
        UNIT_AT = {(name, i): n for n, (name, i, _) in enumerate(UNITS)}

        def unit_sb(n):
            return ring[:, n % NSTREAM, :]

        def unit_arrived(pe, name, i):
            n = UNIT_AT[(name, i)]
            pe.wait_ge(S(f"slot_in{n % NSTREAM}"), 16 * (n // NSTREAM + 1))
            return unit_sb(n)

        STREAMED = [16 * len(range(k, NUNITS, NSTREAM)) for k in range(NSTREAM)] + [0] * 12

        def expert_chunk_sem(u):
            return S(f"slot_in{u}")

        block = ctx.enter_context(nc.Block())

        @block.sync
        def _(sp):
            def stream(n):
                _, _, (src, view) = UNITS[n]
                if n >= NSTREAM:
                    sp.wait_ge(S("unit_used"), n - NSTREAM + 1)
                dst = unit_sb(n)
                if view:
                    dst = dst.rearrange(view[0], **view[1])
                sp.dma_start(dst, src).then_inc(S(f"slot_in{n % NSTREAM}"), 16)

            stream(0)
            sp.dma_start(masks_kept, kept_masks).then_inc(S("small_in"), 16)
            sp.dma_start(vrows[0:8, :], c[0].rearrange("(k p) -> k p", p=P)).then_inc(S("small_in"), 16)
            sp.dma_start(vrows[8:56, :], b_ada[0].rearrange("(k p) -> k p", p=P)).then_inc(S("small_in"), 16)
            sp.dma_start(vrows[56:64, :], g_norm1[0].rearrange("(k p) -> k p", p=P)).then_inc(S("small_in"), 16)
            sp.dma_start(vrows[64:72, :], g_norm2[0].rearrange("(k p) -> k p", p=P)).then_inc(S("small_in"), 16)
            sp.dma_start(vrows[72:120, :], conv_w[0].rearrange("j (k p) -> (j k) p", p=P)).then_inc(S("small_in"), 16)
            sp.dma_start(vrows[120:121, :], g_onorm).then_inc(S("small_in"), 16)
            sp.dma_start(xtok, x[0].rearrange("(t p) d -> p t d", p=P)).then_inc(S("x_in"), 16)
            for n in range(1, NUNITS):
                stream(n)

            def load_gu(e, par, k):
                sp.dma_start(ring[:, par * KD + k, :], w_gate_up[0, e, k * P:(k + 1) * P, :]).then_inc(
                    expert_chunk_sem(par * KD + k), 16)

            def load_dn(e, j):
                sp.dma_start(ring[:, 16 + j, :].rearrange("p (k n) -> p k n", k=2),
                             w_down[0, e, j * 256:(j + 1) * 256, :].rearrange("(k p) n -> p k n", p=P)).then_inc(
                    expert_chunk_sem(16 + j), 16)

            sp.wait_ge(S("oT_ps"), 1)
            for j in range(4):
                load_dn(0, j)
            assert UNIT_AT[("wo_delta", 0)] % NSTREAM == 6 and NUNITS % NSTREAM == 6
            sp.wait_ge(S("y_ps"), 8)
            for k in (6, 7, 0, 1):
                load_gu(0, 0, k)
            sp.wait_ge(S("merged_ready"), 4)
            for k in range(4):
                load_gu(1, 1, k)
            sp.wait_ge(S("out_ps"), 4)
            for k in (2, 3, 4, 5):
                load_gu(0, 0, k)
            for k in range(4, KD):
                load_gu(1, 1, k)
            def next_gu(I, i, par, ks=range(KD)):
                for k in ks:
                    sp.wait_ge(S("gu_used"), I * 16 + (par * KD - 16 + k + 1))
                    load_gu(i * 2 + par, par, k)

            def next_dn(I, i, par):
                for j in range(4):
                    sp.wait_ge(S("dn_used"), I * 8 + (par * 4 - 4 + j + 1))
                    load_dn(i * 2 + par, j)

            def load_round(I0, first):
                if not first:
                    next_gu(I0, 0, 0)
                    next_dn(I0, 0, 0)
                    next_gu(I0, 0, 1)
                with sp.Fori(1, PAIRS - 1) as i:
                    next_gu(I0 + i, i, 0)
                    next_dn(I0 + i + -1, i + -1, 1)
                    next_gu(I0 + i, i, 1)
                    next_dn(I0 + i, i, 0)
                last = PAIRS - 1
                next_gu(I0 + last, last, 0, range(2))
                next_dn(I0 + (last - 1), last - 1, 1)
                next_gu(I0 + last, last, 0, range(2, KD))
                next_dn(I0 + last, last, 0)
                next_gu(I0 + last, last, 1)
                next_dn(I0 + last, last, 1)

            load_round(0, True)

            def one_round(q):
                load_round(q * PAIRS, False)

            n = extra_rounds(sp, one_round)
            sp.wait_ge(S("gu_used"), n * (16 * PAIRS) + (16 * PAIRS - 8))
            sp.dma_start(flat[:, 0:1024], g_final.partition_broadcast(P)).then_inc(S("gfin_in"), 16)

        @block.tensor
        def _(pe):
            def mm(dst, lhsT, rhs, start, stop):
                return pe.matmul(dst, lhsT, rhs, start=start, stop=stop, skip_group_check=True)

            pe.wait_ge(S("small_in"), 112)
            pe.transpose(bank(7, 0, 121), vrows[0:121, :], ident[0:121, 0:121]).then_inc(S("vecs_t"), 1)
            pe.wait_ge(S("x_in"), 16)
            for b in range(4):
                for k in (2 * b, 2 * b + 1):
                    for t in range(TT):
                        last = pe.transpose(bank(b, (k % 2) * T + t * P, P), xtok[:, t, k * P:(k + 1) * P], ident)
                last.then_inc(S("x_t"), 1)

            def ada(part, b, ks=range(KD)):
                for k in ks:
                    w = unit_arrived(pe, f"ada{part}", k)
                    for q in range(4):
                        last = mm(ps[32 * q:32 * q + 32, b, :], cb[:, k, :], w[:, 512 * q:512 * q + 512],
                                  k == 0, k == KD - 1)
                    last.then_inc(S("unit_used"), 1)

            def mod_transposes(part, b):
                pe.wait_ge(S("mod_rows_sb"), part + 1)
                for s in range(4):
                    last = pe.transpose(bank(b, s * P, P), mod_rows[:, s * P:(s + 1) * P], ident)
                last.then_inc(S("mod_cols_ps"), 1)

            pe.wait_ge(S("cb_ready"), 1)
            ada(0, 4, range(5))
            pe.wait_ge(S("xsq_ready"), 1)
            for k in range(KD):
                last = mm(bank(5, 0, T), km("ones"), tmp.rearrange("p (k n) -> p k n", k=KD)[:, k, :],
                          k == 0, k == KD - 1)
            last.then_inc(S("xss_ps"), 1)
            ada(0, 4, range(5, KD))
            mod_transposes(0, 6)
            pe.wait_ge(S("hT_ready"), 2)

            nproj = [0]

            def project(name, u):
                n = nproj[0]
                nproj[0] += 1
                b = n % 2
                w = unit_arrived(pe, name, u).rearrange("p (k n) -> p k n", k=KD)
                if n >= 2:
                    pe.wait_ge(S("proj_taken"), n - 1)
                for m in range(2):
                    for k in range(KD):
                        if name == "fv":
                            lhsT, rhs = hT[:, k, m * P:(m + 1) * P], w[:, k, :]
                        else:
                            lhsT, rhs = w[:, k, m * P:(m + 1) * P], hT[:, k, :]
                        last = mm(bank(b, m * T, T), lhsT, rhs, k == 0, k == KD - 1)
                last.then_inc(S("unit_used"), 1)

            for u in range(6):
                project("dn", u)
            pe.wait_ge(S("narrow_in"), 112)
            for k in range(KD):
                last = mm(ps[0:12, 2, 0:T], wsmall[:, k, :], hT[:, k, :], k == 0, k == KD - 1)
            last.then_inc(S("small_ps"), 1)
            project("fqk", 0)
            pe.wait_ge(S("small_t_ready"), 1)
            for t in range(TT):
                last = pe.transpose(bank(2, 256 + 12 * t, 12), small_t[0:12, t * P:(t + 1) * P], ident[0:12, 0:12])
            last.then_inc(S("small_ps"), 1)
            project("fqk", 1)
            pe.wait_ge(S("early_in"), 16)
            pe.wait_ge(S("g8_ready"), 1)
            for t in range(TT):
                mm(bank(2, 288 + 8 * t, 8), em("cum_chunk"), g8[:, t, :], True, True)
                mm(bank(2, 304 + 8 * t, 8), em("suffix_chunk"), g8[:, t, :], True, True)
            mm(bank(2, 320, 8), em("cum_all_ones", P), g8[:, 0, :], True, True)
            mm(bank(2, 328, 8), em("cum_all_ones", P), g8[:, 1, :], True, False)
            mm(bank(2, 328, 8), km("ones"), g8[:, 0, :], False, True).then_inc(S("cums_ps"), 1)
            pe.wait_ge(S("gb_ready"), 1)
            for h in range(H):
                for t in range(TT):
                    last = mm(bank(3 + h // 2, (h % 2) * T + t * P, P), gb[:, t, h, :], em("cum_chunk"), True, True)
            last.then_inc(S("cums_ps"), 1)
            for h in range(H):
                mm(bank(5 + h // 2, (h % 2) * T, T), gb[:, 0, H + h, :], em("cum_all_ones", 2 * P), True, False)
                last = mm(bank(5 + h // 2, (h % 2) * T + P, P), gb[:, 1, H + h, :], em("cum_all_ones", P), False, True)
            last.then_inc(S("cums_ps"), 1)
            project("fqk", 2)
            project("fqk", 3)
            for half in range(2):
                pe.wait_ge(S("qk_sq_ready"), half + 1)
                if half == 0:
                    pe.wait_ge(S("cums_taken"), 1)
                else:
                    pe.wait_ge(S("qk_ss_taken"), 1)
                for h in range(H):
                    last = mm(bank((2, 7)[h // 2], (h % 2) * T, T), km("ones"),
                              tmp[:, half * 1024 + h * T:half * 1024 + (h + 1) * T], True, True)
                last.then_inc(S("qk_ss_ps"), 1)
                project("fv", half)
            pe.wait_ge(S("unit_qk"), 2)
            pe.wait_ge(S("qk_ss_taken"), 2)
            for t in range(TT):
                for h in range(H):
                    last = pe.transpose(bank((2, 7)[t], h * P, P), kn[:, h, t * P:(t + 1) * P], ident)
            last.then_inc(S("tok_ps"), 1)
            pe.wait_ge(S("dec_ready"), 1)
            pe.wait_ge(S("exg_ready"), 1)
            for t in range(TT):
                for h in range(H):
                    last = pe.transpose(bank(3 + t, h * P, P), vT[:, h, t * P:(t + 1) * P], ident)
            last.then_inc(S("tok_ps"), 1)
            project("z", 0)
            project("z", 1)
            pe.wait_ge(S("ktok_taken"), 1)
            for t in range(TT):
                for h in range(H):
                    a = kn[:, h, t * P:(t + 1) * P]
                    last = mm(bank((2, 7)[t], h * P, P), a, a, True, True)
            last.then_inc(S("pairs_ps"), 1)
            pe.wait_ge(S("vtok_taken"), 1)
            pe.wait_ge(S("unit_qk"), 1)
            for t in range(TT):
                for h in range(H):
                    last = mm(bank(3 + t, h * P, P), kn[:, h, t * P:(t + 1) * P], qn[:, h, t * P:(t + 1) * P],
                              True, True)
            last.then_inc(S("pairs_ps"), 1)
            pe.wait_ge(S("rowF_taken"), 1)
            ada(1, 5)
            mod_transposes(1, 6)
            pe.wait_ge(S("X1_ready"), 1)
            for t in range(TT):
                for h in range(H):
                    last = pe.transpose(bank((2, 7)[t], h * P, P), Xm[:, t, h, :], ident)
            last.then_inc(S("U1_ps"), 1)
            project("gates", 0)
            pe.wait_ge(S("mod_cols_taken"), 2)
            pe.wait_ge(S("attn_ready"), 1)
            for s in range(1, LEVELS):
                pe.wait_ge(S("U_ready"), s)
                pe.wait_ge(S("M_ready"), s)
                for t in range(TT):
                    for h in range(H):
                        last = mm(bank((2, 7)[t], h * P, P), Mm[:, t, h, :], Um[:, t, h, :], True, True)
                last.then_inc(S("R_ps"), 1)
                project("gates", s)
                pe.wait_ge(S("R_ready"), s)
                for t in range(TT):
                    for h in range(H):
                        last = mm(bank(5 + t, h * P, P), Xm[:, t, h, :], Rm[:, t, h, :], True, True)
                if s < LEVELS - 1:
                    for t in range(TT):
                        for h in range(H):
                            last = mm(bank(3 + t, h * P, P), Rm[:, t, h, :], Xm[:, t, h, :], True, True)
                last.then_inc(S("XMX_ps"), 1)
            project("gates", LEVELS)
            pe.wait_ge(S("U_ready"), LEVELS)
            for t in range(TT):
                for h in range(H):
                    last = mm(bank((2, 7)[t], h * P, P), Um[:, t, h, :], vb[:, t, h, :], True, True)
            last.then_inc(S("uw_ps"), 1)
            for t in range(TT):
                for h in range(H):
                    last = mm(bank(3 + t, h * P, P), kbx[:, t, h, :], Um[:, t, h, :], True, True)
            last.then_inc(S("uw_ps"), 1)
            project("gates", LEVELS + 1)
            pe.wait_ge(S("proj_taken"), nproj[0])
            for h in range(H):
                q, k = fqk[:, h, :], fqk[:, H + h, :]
                mm(bank(5, h * P, P), q[:, 0:P], k[:, 0:P], True, True)
                last = mm(bank((6, 0)[h // 2], (h % 2) * T, T), q[:, P:T], k, True, True)
            last.then_inc(S("fox_ps"), 1)
            pe.wait_ge(S("uw_taken"), 1)
            pe.wait_ge(S("uw_taken"), 2)
            pe.wait_ge(S("qd_ready"), 1)
            for n in range(NCH):
                t, r = n // 2, (n % 2) * CH
                rows = slice(r, r + CH)
                toks = slice(n * CH, (n + 1) * CH)
                pe.wait_ge(S("state_ready"), n + 1)
                for h in range(H):
                    last = mm(ps[rows, 2, h * P:(h + 1) * P], w_t[:, t, h, rows], state[:, h, :], True, True)
                last.then_inc(S("ws_ps"), 1)
                for h in range(H):
                    mm(ps[rows, 3 + t, h * P:(h + 1) * P], qn[:, h, toks], state[:, h, :], h == 0, False)
                pe.wait_ge(S("vnew_ready"), n + 1)
                if n < NCH - 1:
                    for h in range(H):
                        last = mm(bank(7, h * P, P), kd[rows, t, h, :], vnew[rows, t, h, :], True, True)
                    last.then_inc(S("ds_ps"), 1)
                if n % 2:
                    for h in range(H):
                        last = mm(bank(3 + t, h * P, P), attn_t[:, t, h, :], vnew[:, t, h, :], False, True)
                    last.then_inc(S("o_ps"), 1)
                if n == 0:
                    pe.wait_ge(S("fox_p_ready"), 1)
                    for h in range(H):
                        pe.transpose(bank((6, 0)[h // 2], (h % 2) * T, P), fox_p0[:, h, :], ident)
                        pe.transpose(bank((6, 0)[h // 2], (h % 2) * T + P, P), fox_p1[:, h, 0:P], ident)
                        last = pe.transpose(bank(5, h * P, P), fox_p1[:, h, P:T], ident)
                    last.then_inc(S("fox_ps"), 1)
                if n == 1:
                    pe.wait_ge(S("fox_pt_ready"), 2)
                    for h in range(H):
                        b = (1, 5)[h // 2]
                        mm(bank(b, (h % 2) * T, T), fv[:, 0, h * P:(h + 1) * P], fox_pt0[:, h, :], True, False)
                        last = mm(bank(b, (h % 2) * T + P, P), fv[:, 1, h * P:(h + 1) * P], fox_pt1[:, h, :],
                                  False, True)
                    last.then_inc(S("fox_ps"), 1)
            pe.wait_ge(S("on_ready"), 1)
            for h in range(H):
                for t in range(TT):
                    last = pe.transpose(bank((2, 7)[h // 2], (h % 2) * T + t * P, P), o_sb[:, t, h, :], ident)
            last.then_inc(S("oT_ps"), 1)
            ada(2, 6)
            mod_transposes(2, 0)
            pe.wait_ge(S("obT_ready"), 1)
            pe.wait_ge(S("oaT_ready"), 1)
            wd = [unit_arrived(pe, "wo_delta", u).rearrange("p (k n) -> p k n", k=2) for u in range(2)]
            wf = [unit_arrived(pe, "wo_fox", u).rearrange("p (k n) -> p k n", k=2) for u in range(2)]
            for g in range(4):
                for br, (w, o) in enumerate(((wd, oaT), (wf, obT))):
                    b = ((1, 2), (3, 4))[g % 2][br]
                    if g >= 2:
                        pe.wait_ge(S("y_taken"), 2 * (g - 2) + br + 1)
                    for m in (2 * g, 2 * g + 1):
                        for k in range(H):
                            last = mm(bank(b, (m % 2) * T, T), w[k // 2][:, k % 2, m * P:(m + 1) * P], o[:, k, :],
                                      k == 0, k == H - 1)
                    last.then_inc(S("y_ps"), 1)
            wo = [unit_arrived(pe, "w_out", u).rearrange("p (k n) -> p k n", k=2) for u in range(4)]
            pe.wait_ge(S("merged_ready"), 4)
            for g in range(4):
                for m in (2 * g, 2 * g + 1):
                    for k in range(KD):
                        last = mm(bank((5, 6, 7, 4)[g], (m % 2) * T, T), wo[k // 2][:, k % 2, m * P:(m + 1) * P],
                                  merged[:, k, :], k == 0, k == KD - 1)
                last.then_inc(S("out_ps"), 1)
            for k in range(KD):
                if k % 2 == 0:
                    pe.wait_ge(S("xsq_ready"), k // 2 + 2)
                last = mm(bank(5, 0, T), km("ones"), x1sq[:, k, :], k == 0, k == KD - 1)
            last.then_inc(S("xss_ps"), 1)
            pe.wait_ge(S("gt2b_ready"), 1)
            for k in range(KD):
                last = mm(bank(6 + k // 4, (k % 4) * P, P), gt2b[:, k, :], ident, True, True)
            last.then_inc(S("gt2_ps"), 1)
            for t in range(TT):
                for k in range(KD):
                    last = mm(bank(2 * t + k // 4, (k % 4) * P, P), xT[:, k, t * P:(t + 1) * P], ident,
                              k % 4 == 0, False)
            last.then_inc(S("x1_summed"), 1)
            for k in range(KD):
                if k % 4 == 0:
                    pe.wait_ge(S("h2T_low" if k == 0 else "h2T_high"), 1)
                last = mm(ps[0:E, 5, 0:T], wrout[:, k, :], merged[:, k, :], k == 0, k == KD - 1)
            last.then_inc(S("logits_ps"), 1)
            for t in range(TT):
                if t == 0:
                    pe.wait_ge(S("gt2_taken"), 1)
                else:
                    pe.wait_ge(S("h2tok_taken"), 1)
                for k in range(KD):
                    last = pe.transpose(bank(6 + k // 4, (k % 4) * P, P), merged[:, k, t * P:(t + 1) * P], ident)
                last.then_inc(S("h2tok_ps"), 1)
                if t == 0:
                    pe.wait_ge(S("logits_t_ready"), 1)
                    for tt in range(TT):
                        la = pe.transpose(bank(5, 256 + E * tt, E), small_t[0:E, tt * P:(tt + 1) * P],
                                          ident[0:E, 0:E])
                    la.then_inc(S("logits_ps"), 1)
            pe.wait_ge(S("chosen_ready"), 1)
            mm(bank(4, 0, E), km("before"), chosen[:, 0, :], True, True)
            mm(bank(4, E, E), km("before"), chosen[:, 1, :], True, False)
            mm(bank(4, E, E), km("ones"), chosen[:, 0, :], False, True)
            mm(bank(4, 2 * E, E), km("ones"), chosen[:, 0, :], True, False)
            mm(bank(4, 2 * E, E), km("ones"), chosen[:, 1, :], False, True).then_inc(S("route_ps"), 1)

            def open_sums():
                pe.wait_ge(S("gate_w_ready"), 1)
                for t in range(TT):
                    last = pe.transpose(ps[0:E, 7, t * P:(t + 1) * P], gate_w[:, t, :], ident)
                last.then_inc(S("route_ps"), 1)
                pe.wait_ge(S("gates_t_ready"), 1)
                pe.wait_ge(S("bdown_ready"), 1)
                for t in range(TT):
                    for d in range(2):
                        last = mm(bank(2 * t + d), scat[:, t * P:(t + 1) * P], ypair[:, d * 512:(d + 1) * 512],
                                  False, False)
                last.then_inc(S("bdown_used"), 1)

            def gather(n):
                pe.wait_ge(S("onehot_ready"), n)
                for half in range(2):
                    b = 7 - half
                    for kk in range(4):
                        k = 4 * half + kk
                        for t in range(TT):
                            last = mm(bank(b, kk * P, P), h2tok[:, t, k * P:(k + 1) * P], onehot[:, t, :],
                                      t == 0, t == TT - 1)
                    last.then_inc(S("xg_ps"), 1)

            def gate_up(i, par):
                e = i * 2 + par
                pe.wait_ge(S("sel_ready"), e + 1)
                wait_past_first(pe, S("gate_ready"), e)
                wait_past_first(pe, S("up_ready"), e)
                for q in range(4):
                    mm(ps[64 * (q % 2):64 * (q % 2) + 64, 4 + q // 2, :], sel[:, par, q, :], bias_gu, True, False)
                for k in range(KD):
                    pe.wait_ge(expert_chunk_sem(par * KD + k), i * 16 + (16 + STREAMED[par * KD + k]))
                    for q in range(4):
                        last = mm(ps[64 * (q % 2):64 * (q % 2) + 64, 4 + q // 2, :], xg[:, k, par * 64:par * 64 + 64],
                                  ring[:, par * KD + k, 512 * q:512 * q + 512], False, k == KD - 1)
                    last.then_inc(S("gu_used"), 1)

            def act_transposes(i, par):
                pe.wait_ge(S("act_ready"), i * 2 + (par + 1))
                for j in range(4):
                    last = pe.transpose(bank(7, j * P, P), gate_a[:, j * P:(j + 1) * P], ident)
                last.then_inc(S("act_t_ps"), 1)

            def down(i, par):
                e = i * 2 + par
                pe.wait_ge(S("act_t_ready"), e + 1)
                for j in range(4):
                    pe.wait_ge(expert_chunk_sem(16 + j), i * 32 + (par * 16 + 16))
                    for kk in range(2):
                        k = 2 * j + kk
                        lhsT = act_t[:, (k % 4) * P + (k // 4) * 64:(k % 4) * P + (k // 4) * 64 + 64]
                        for d in range(2):
                            last = mm(ps[64 * d:64 * d + 64, 6, :], lhsT,
                                      ring[:, 16 + j, kk * 1024 + d * 512:kk * 1024 + d * 512 + 512],
                                      k == 0, k == KD - 1)
                    last.then_inc(S("dn_used"), 1)

            def scat_transposes():
                for t in range(TT):
                    last = pe.transpose(bank(7, t * P, P), gated[:, t, :], ident)
                last.then_inc(S("scat_ps"), 1)

            def scatter(stop=False):
                for t in range(TT):
                    for d in range(2):
                        last = mm(bank(2 * t + d), scat[:, t * P:(t + 1) * P], ypair[:, d * 512:(d + 1) * 512],
                                  False, stop)
                    if stop and t == 0:
                        last.then_inc(S("half_summed"), 1)
                last.then_inc(S("scattered"), 1)

            pe.wait_ge(S("slots_taken"), 1)
            pe.wait_ge(S("h2tok_taken"), 2)
            pe.wait_ge(S("bias_in"), 64)

            def pair(i, first, more, opening=False):
                gate_up(i, 0)
                if opening:
                    open_sums()
                if not first:
                    pe.wait_ge(S("y_moved"), i * 4)
                    scatter()
                act_transposes(i, 0)
                down(i, 0)
                pe.wait_ge(S("gated_ready"), i + 1)
                scat_transposes()
                gate_up(i, 1)
                if more:
                    pe.wait_ge(S("y_moved"), i * 4 + 2)
                    pe.wait_ge(S("scat_ready"), i + 1)
                    gather(i + 2)
                    pe.wait_ge(S("xg_ready"), i * 2 + 4)
                act_transposes(i, 1)
                if not more:
                    pe.wait_ge(S("y_moved"), i * 4 + 2)
                down(i, 1)

            def one_round(q):
                I0 = q * PAIRS
                gather(I0 + 1)
                pe.wait_ge(S("xg_ready"), I0 * 2 + 2)
                pair(I0, True, True, opening=isinstance(q, int))
                with pe.Fori(1, PAIRS - 1) as i:
                    pair(I0 + i, False, True)
                pair(I0 + (PAIRS - 1), False, False)
                pe.wait_ge(S("y_moved"), I0 * 4 + 4 * PAIRS)
                pe.wait_ge(S("scat_ready"), I0 + PAIRS)
                scatter(True)

            one_round(0)
            extra_rounds(pe, one_round)

        @block.scalar
        def _(act):
            chain = [0]

            def link(ins):
                chain[0] += 1
                ins.then_inc(S("act_chain"), 1)
                act.wait_ge(S("act_chain"), chain[0])

            A = act.activation
            for dst, src in ((alog_b, a_log[0]), (dt_b, dt_bias[0]), (fg_b, b_fgate[0]), (brout, b_router[0])):
                act.dma_start(dst, src.partition_broadcast(P)).then_inc(S("narrow_in"), 16)
            act.dma_start(wsmall[:, :, 0:8], win3[:, :, COL_SMALL:COL_SMALL + 8]).then_inc(S("narrow_in"), 16)
            act.dma_start(wsmall[:, :, 8:12], win3[:, :, COL_F:COL_F + 4]).then_inc(S("narrow_in"), 16)

            xTf = xT.rearrange("p k n -> p (k n)")
            act.dma_start(wrout, w_router[0].rearrange("(k p) e -> p k e", p=P)).then_inc(S("narrow_in"), 16)
            act.wait_ge(S("x_t"), 4)
            act.dma_start(masks_early, early_masks).then_inc(S("early_in"), 16)
            link(A(xTf[:, 1024:2048].rearrange("p (b n) -> p b n", b=2), ps[:, 2:4, :], ACT.Copy))
            act.wait_ge(S("xT_half"), 1)
            act.wait_ge(S("vecs_t"), 1)
            A(tmp, xTf, ACT.Square).then_inc(S("xsq_ready"), 1)
            act.wait_ge(S("xss_ps"), 1)
            link(A(rstd, bank(5, 0, T), ACT.Ln, scale=1.0 / D, bias=km("rms_eps")))
            A(rstd, rstd, ACT.Exp, scale=-0.5).then_inc(S("rstd_ready"), 1)
            act.wait_ge(S("A1_ready"), 1)
            for k in range(4, KD):
                last = A(hT[:, k, :], hT[:, k, :], ACT.Identity, scale=A1[:, k:k + 1], bias=mod[:, k:k + 1])
            last.then_inc(S("hT_ready"), 1)

            nproj = [0]

            def take(name, u):
                n = nproj[0]
                nproj[0] += 1
                act.wait_ge(S("unit_used"), UNIT_AT[(name, u)] + 1)
                src = bank(n % 2).rearrange("p (m n) -> p m n", m=2)
                f = {"z": ACT.Silu, "gates": ACT.Sigmoid}.get(name, ACT.Copy)
                if name == "fv":
                    dst = fv[:, :, 256 * u:256 * u + 256]
                elif name == "dn":
                    dst = raw[:, 2 * u:2 * u + 2, 3:RAW]
                else:
                    dst = {"fqk": fqk, "z": zT, "gates": gates}[name][:, 2 * u:2 * u + 2, :]
                A(dst, src, f).then_inc(S("proj_taken"), 1)

            def silu_qkv(u):
                act.wait_ge(S("conv_ready"), u + 1)
                return A(qkv[:, 2 * u:2 * u + 2, :], qkv[:, 2 * u:2 * u + 2, :], ACT.Silu)

            for u in range(6):
                take("dn", u)
            act.wait_ge(S("small_ps"), 1)
            A(small_t[0:12, :], ps[0:12, 2, 0:T], ACT.Copy).then_inc(S("small_t_ready"), 1)
            for u in range(3):
                silu_qkv(u)
            take("fqk", 0)
            act.wait_ge(S("s12_ready"), 1)
            A(beta, s12[:, :, 0:4], ACT.Sigmoid).then_inc(S("beta_ready"), 1)
            for u in range(3, 5):
                silu_qkv(u)
            link(silu_qkv(5))
            act.wait_ge(S("y8_ready"), 1)
            A(ea, alog_b, ACT.Exp)
            A(e8, ab8, ACT.Exp, scale=-1.0).then_inc(S("e8_ready"), 1)
            take("fqk", 1)
            act.wait_ge(S("u8_ready"), 1)
            A(l8, u8, ACT.Ln).then_inc(S("l8_ready"), 1)
            for half in range(2):
                A(tmp[:, half * 1024:(half + 1) * 1024],
                  qkv[:, 4 * half:4 * half + 4, :].rearrange("p h n -> p (h n)"), ACT.Square).then_inc(
                    S("qk_sq_ready"), 1)
            take("fqk", 2)
            take("fqk", 3)
            act.wait_ge(S("cums_ps"), 2)
            link(A(exg.rearrange("p (b h) n -> p b (h n)", b=2), ps[:, 3:5, :], ACT.Exp))
            A(eg, exg[:, :, CH - 1:T:CH], ACT.Copy).then_inc(S("exg_ready"), 1)
            for half in range(2):
                act.wait_ge(S("qk_ss_ps"), half + 1)
                dst = tmp[:, half * 1024:(half + 1) * 1024]
                link(A(dst[:, 0:512], bank(2), ACT.Ln, bias=km("rms_eps")))
                A(dst[:, 512:1024], bank(7), ACT.Ln, bias=km("rms_eps")).then_inc(S("qk_ss_taken"), 1)
                act.wait_ge(S("qk_ss_taken"), half + 1)
                A(dst, dst, ACT.Exp, scale=-0.5).then_inc(S("qk_rstd"), 1)
                take("fv", half)
            act.wait_ge(S("cums_taken"), 1)
            link(A(bx, cums[:, 0, :, 0:H], ACT.Exp))
            A(kdf, cums[:, 1, :, 0:H], ACT.Exp).then_inc(S("bx_ready"), 1)
            act.wait_ge(S("dec_ready"), 1)
            A(dec_l, dec_l, ACT.Exp, scale=-1.0)
            A(dec_a, dec_a, ACT.Exp).then_inc(S("decay_ready"), 1)
            take("z", 0)
            take("z", 1)
            take("gates", 0)
            for s in range(1, LEVELS):
                act.wait_ge(S("R_ps"), s)
                A(Rm[:, 0], bank(2).rearrange("p (h n) -> p h n", h=H), ACT.Copy)
                A(Rm[:, 1], bank(7).rearrange("p (h n) -> p h n", h=H), ACT.Copy).then_inc(S("R_ready"), 1)
                take("gates", s)
            take("gates", LEVELS)
            act.wait_ge(S("uw_ps"), 1)
            A(u_sb[:, 0], bank(2).rearrange("p (h n) -> p h n", h=H), ACT.Copy)
            A(u_sb[:, 1], bank(7).rearrange("p (h n) -> p h n", h=H), ACT.Copy).then_inc(S("uw_taken"), 1)
            act.wait_ge(S("uw_ps"), 2)
            A(w_t, ps[:, 3:5, :].rearrange("p t (h n) -> p t h n", h=H), ACT.Copy).then_inc(S("uw_taken"), 1)
            take("gates", LEVELS + 1)
            for t in range(TT):
                act.wait_ge(S("fox_max_ready"), t + 1)
                for h in range(H):
                    p = (fox_p0, fox_p1)[t][:, h, :]
                    last = A(p, p, ACT.Exp, bias=fmax[:, t, h:h + 1], accum_out=fsum[:, t, h:h + 1])
                last.then_inc(S("fox_exp"), 1)
            act.wait_ge(S("fox_ps"), 2)
            act.wait_ge(S("fox_s_taken"), 1)
            A(fox_pt0[:, 0:2, :], ps[:, 6, :].rearrange("p (h n) -> p h n", h=2), ACT.Copy)
            A(fox_pt0[:, 2:4, :], ps[:, 0, :].rearrange("p (h n) -> p h n", h=2), ACT.Copy).then_inc(
                S("fox_pt_ready"), 1)
            A(fox_pt1, bank(5).rearrange("p (h n) -> p h n", h=H), ACT.Copy).then_inc(S("fox_pt_ready"), 1)
            act.wait_ge(S("fox_ps"), 3)
            A(obT[:, 0:2, :], ps[:, 1, :].rearrange("p (h n) -> p h n", h=2), ACT.Copy)
            A(obT[:, 2:4, :], ps[:, 5, :].rearrange("p (h n) -> p h n", h=2), ACT.Copy).then_inc(S("obT_ready"), 1)
            for t in range(TT):
                act.wait_ge(S("o_ps"), t + 1)
                for h in range(H):
                    last = A(u_sb[:, t, h, :], bank(3 + t, h * P, P), ACT.Square,
                             accum_out=oss[:, t, h:h + 1])
            link(last)
            link(A(oss, oss, ACT.Ln, scale=1.0 / HD, bias=km("rms_eps")))
            A(oss, oss, ACT.Exp, scale=-0.5).then_inc(S("oss_ready"), 1)
            for g in range(4):
                act.wait_ge(S("x1_ready"), g + 1)
                A(x1sq[:, 2 * g:2 * g + 2, :], xT[:, 2 * g:2 * g + 2, :], ACT.Square).then_inc(S("xsq_ready"), 1)
            act.wait_ge(S("xss_ps"), 2)
            link(A(rs2, bank(5, 0, T), ACT.Ln, scale=1.0 / D, bias=km("rms_eps")))
            A(rs2, rs2, ACT.Exp, scale=-0.5).then_inc(S("rstd_ready"), 1)
            act.wait_ge(S("h2_scaled"), 1)
            for k in range(4):
                last = A(merged[:, k, :], merged[:, k, :], ACT.Identity, scale=A2[:, k:k + 1],
                         bias=mod[:, 24 + k:25 + k])
            last.then_inc(S("h2T_low"), 1)
            act.wait_ge(S("gt2_ps"), 1)
            A(gt2_row.rearrange("p (b n) -> p b n", b=2), ps[:, 6:8, :], ACT.Copy).then_inc(S("gt2_taken"), 1)
            act.wait_ge(S("logits_ps"), 1)
            A(small_t[0:E, :], ps[0:E, 5, 0:T], ACT.Copy).then_inc(S("logits_t_ready"), 1)
            for t in range(TT):
                act.wait_ge(S("h2tok_ps"), t + 1)
                A(h2tok[:, t, :].rearrange("p (b n) -> p b n", b=2), ps[:, 6:8, :], ACT.Copy).then_inc(
                    S("h2tok_taken"), 1)
            act.wait_ge(S("top_ready"), 1)
            for t in range(TT):
                last = A(top8[:, t, 0:TOPK], top8[:, t, 0:TOPK], ACT.Exp, bias=ssum[:, t:t + 1],
                         accum_out=ssum[:, 2 + t:3 + t])
            last.then_inc(S("top_exp"), 1)

            def take_xg(n):
                act.wait_ge(S("xg_ps"), n)
                A(xg[:, 0:4, :], bank(7).rearrange("p (k n) -> p k n", k=4), ACT.Copy).then_inc(S("xg_ready"), 1)

            def expert(i, par, more):
                e = i * 2 + par
                act.wait_ge(S("gate_ready"), e + 1)
                A(sig_a, gate_a, ACT.Sigmoid, scale=ALPHA).then_inc(S("sig_ready"), 1)
                if par == 1 and more:
                    take_xg(i * 2 + 3)
                act.wait_ge(S("act_t_ps"), e + 1)
                A(act_t, bank(7), ACT.Copy).then_inc(S("act_t_ready"), 1)

            def one_round(q):
                I0 = q * PAIRS
                take_xg(I0 * 2 + 1)
                for par in range(2):
                    expert(I0, par, True)
                with act.Fori(1, PAIRS - 1) as i:
                    for par in range(2):
                        expert(I0 + i, par, True)
                for par in range(2):
                    expert(I0 + (PAIRS - 1), par, False)

            one_round(0)
            nr = extra_rounds(act, one_round)
            A(ssum[:, 0:1], km("rms_eps"), ACT.Sqrt)
            for t in range(TT):
                if t == 0:
                    act.wait_ge(S("half_summed"), nr + 1)
                else:
                    act.wait_ge(S("scattered"), nr * PAIRS + PAIRS)
                link(A(x2sq[:, t, :].rearrange("p (b n) -> p b n", b=2), ps[:, 2 * t:2 * t + 2, :], ACT.Square,
                       accum_out=oss[:, 0, t:t + 1]))
                A(oss[:, 1, t:t + 1], oss[:, 0, t:t + 1], ACT.Sqrt, scale=1.0 / D, bias=km("rms_eps")).then_inc(
                    S("root_ready"), 1)
            for t in range(TT):
                act.wait_ge(S("out_sb"), t + 1)
                act.dma_start(out[0, t * P:(t + 1) * P, :], x2[:, t, :]).then_inc(S("out_done"), 16)
            act.wait_ge(S("out_done"), 16 * TT)

        @block.vector
        def _(dve):
            chain = [0]

            def link(ins):
                chain[0] += 1
                ins.then_inc(S("dve_chain"), 1)
                dve.wait_ge(S("dve_chain"), chain[0])

            TTn, TS, STT, CP = dve.tensor_tensor, dve.tensor_scalar, dve.scalar_tensor_tensor, dve.tensor_copy
            xTf = xT.rearrange("p k n -> p (k n)")
            dve.wait_ge(S("vecs_t"), 1)
            link(CP(vecs, bank(7, 0, 121)))
            CP(cb, vecs[:, 0:KD].unsqueeze(2).to_broadcast([P, KD, 32])).then_inc(S("cb_ready"), 1)
            dve.wait_ge(S("x_t"), 2)
            CP(xTf[:, 0:1024].rearrange("p (b n) -> p b n", b=2), ps[:, 0:2, :]).then_inc(S("xT_half"), 1)
            dve.wait_ge(S("xsq_ready"), 1)
            dve.wait_ge(S("rstd_ready"), 1)
            link(TTn(hT, xT, rstd.unsqueeze(1).to_broadcast([P, KD, T]), ALU.mult))
            S_mod = [0]

            def take_mod(part, b):
                dve.wait_ge(S("mod_cols_ps"), part + 1)
                m = mod[:, 16 * part:16 * part + 16].rearrange("p (i s) -> p i s", i=4)
                src = bank(b).rearrange("p (s i r) -> p i s r", s=4, i=4)[:, :, :, 0]
                bb = vec("b_ada", 16 * part, 16).rearrange("p (i s) -> p i s", i=4)
                ins = TTn(m, src, bb, ALU.add)
                ins.then_inc(S("mod_cols_taken"), 1)
                dve.wait_ge(S("mod_cols_taken"), part + 1)

            def take_mod_rows(part, b):
                dve.wait_ge(S("unit_used"), UNIT_AT[(f"ada{part}", KD - 1)] + 1)
                CP(mod_rows, bank(b)).then_inc(S("mod_rows_sb"), 1)

            take_mod_rows(0, 4)
            take_mod(0, 6)
            ins = STT(A1, mod[:, 8:16], 1.0, vec("g1", 0, KD), ALU.add, ALU.mult)
            ins.then_inc(S("A1_ready"), 1)
            dve.wait_ge(S("A1_ready"), 1)
            for k in range(4):
                last = TS(hT[:, k, :], hT[:, k, :], A1[:, k:k + 1], mod[:, k:k + 1], ALU.mult, ALU.add)
            last.then_inc(S("hT_ready"), 1)
            dve.wait_ge(S("zeroed"), 1)
            for u in range(6):
                dve.wait_ge(S("proj_taken"), u + 1)
                for j in range(4):
                    for m in (2 * u, 2 * u + 1):
                        w = vec("conv", 12 * j + m)
                        if j == 0:
                            last = TS(qkv[:, m, :], raw[:, m, 0:T], w, None, ALU.mult)
                        else:
                            last = STT(qkv[:, m, :], raw[:, m, j:j + T], w, qkv[:, m, :], ALU.mult, ALU.add)
                    if j < 3:
                        link(last)
                last.then_inc(S("conv_ready"), 1)
            dve.wait_ge(S("conv_ready"), 6)
            dve.wait_ge(S("small_ps"), 2)
            ins = CP(s12, bank(2, 256, 24).rearrange("p (t c) -> p t c", t=TT))
            ins.then_inc(S("s12_ready"), 1)
            dve.wait_ge(S("s12_ready"), 1)
            dve.wait_ge(S("narrow_in"), 112)
            TTn(y8[:, :, 0:4], s12[:, :, 4:8], dt_b.unsqueeze(1).to_broadcast([P, TT, H]), ALU.add)
            link(STT(y8[:, :, 4:8], s12[:, :, 8:12], -1.0, fg_b.unsqueeze(1).to_broadcast([P, TT, H]),
                     ALU.mult, ALU.subtract))
            STT(ab8, y8, -1.0, y8, ALU.mult, ALU.max).then_inc(S("y8_ready"), 1)
            dve.wait_ge(S("e8_ready"), 1)
            ins = TS(u8, e8, 1.0, None, ALU.add)
            ins.then_inc(S("u8_ready"), 1)
            dve.wait_ge(S("u8_ready"), 1)
            link(STT(ab8, u8, 1.0, e8, ALU.subtract, ALU.subtract))
            link(dve.reciprocal(g8, u8))
            link(TTn(g8, g8, ab8, ALU.mult))
            link(STT(y8, y8, 0.0, g8, ALU.max, ALU.subtract))
            dve.wait_ge(S("l8_ready"), 1)
            link(TTn(y8, y8, l8, ALU.add))
            STT(g8[:, :, 0:4], y8[:, :, 0:4], -1.0, ea.unsqueeze(1).to_broadcast([P, TT, H]), ALU.mult, ALU.mult)
            ins = TS(g8[:, :, 4:8], y8[:, :, 4:8], -1.0, None, ALU.mult)
            ins.then_inc(S("g8_ready"), 1)
            dve.wait_ge(S("g8_ready"), 1)
            CP(gb, g8.unsqueeze(3).to_broadcast([P, TT, 2 * H, P])).then_inc(S("gb_ready"), 1)
            dve.wait_ge(S("cums_ps"), 1)
            ins = CP(cums.rearrange("p a t h -> p (a t h)"), bank(2, 288, 48))
            ins.then_inc(S("cums_taken"), 1)
            dve.wait_ge(S("cums_taken"), 1)
            for half in range(2):
                dve.wait_ge(S("qk_rstd"), half + 1)
                v = qkv[:, 4 * half:4 * half + 4, :].rearrange("p h n -> p (h n)")
                r = tmp[:, half * 1024:(half + 1) * 1024]
                if half == 0:
                    STT(v, v, SCALE, r, ALU.mult, ALU.mult).then_inc(S("unit_qk"), 1)
                else:
                    TTn(v, v, r, ALU.mult).then_inc(S("unit_qk"), 1)
            dve.wait_ge(S("unit_qk"), 2)
            dve.wait_ge(S("cums_ps"), 2)
            for t in range(TT):
                for h in range(H):
                    row = bank(3 + h // 2, (h % 2) * T + t * P, P)
                    STT(dec_l[:, t, h, :], row, cums[:, 0, t, h:h + 1], em("outside_strict"), ALU.subtract, ALU.add)
                    last = STT(dec_a[:, t, h, :], row, cums[:, 0, t, h:h + 1], em("outside_incl_t"),
                               ALU.subtract, ALU.subtract)
            last.then_inc(S("dec_ready"), 1)
            dve.wait_ge(S("exg_ready"), 1)
            dve.wait_ge(S("cums_ps"), 3)
            for h in range(H):
                b, a = 5 + h // 2, (h % 2) * T
                STT(fox_e0[:, h, :], bank(b, a, P), cums[:, 2, 0, H + h:H + h + 1], em("fox_outside"),
                    ALU.subtract, ALU.add)
                last = STT(fox_e1[:, h, :], bank(b, a, T), cums[:, 2, 1, H + h:H + h + 1], em("fox_open", 2 * P),
                           ALU.subtract, ALU.add)
            last.then_inc(S("rowF_taken"), 1)
            dve.wait_ge(S("rowF_taken"), 1)
            dve.wait_ge(S("bx_ready"), 1)
            dve.wait_ge(S("beta_ready"), 1)
            link(TTn(bx, bx, beta, ALU.mult))

            def per_head(dst, b, f):
                return TTn(dst, bank(b).rearrange("p (h n) -> p h n", h=H), f.unsqueeze(2).to_broadcast([P, H, P]),
                           ALU.mult)

            dve.wait_ge(S("tok_ps"), 1)
            for t in range(TT):
                per_head(kbx[:, t], (2, 7)[t], bx[:, t, :])
                last = per_head(kd[:, t], (2, 7)[t], kdf[:, t, :])
            last.then_inc(S("ktok_taken"), 1)
            dve.wait_ge(S("tok_ps"), 2)
            for t in range(TT):
                last = per_head(vb[:, t], 3 + t, beta[:, t, :])
            last.then_inc(S("vtok_taken"), 1)
            dve.wait_ge(S("pairs_ps"), 1)
            dve.wait_ge(S("decay_ready"), 1)
            for t in range(TT):
                for h in range(H):
                    last = STT(Lm[:, t, h, :], bank((2, 7)[t], h * P, P), beta[:, t, h:h + 1], dec_l[:, t, h, :],
                               ALU.mult, ALU.mult)
            link(last)

            def level(s):
                for t in range(TT):
                    last = TTn(Mm[:, t], Lm[:, t], em(f"level{s}").unsqueeze(1).to_broadcast([P, H, P]), ALU.mult)
                return last

            link(level(0))
            for t in range(TT):
                last = TTn(Xm[:, t], ident.unsqueeze(1).to_broadcast([P, H, P]), Mm[:, t], ALU.subtract)
            last.then_inc(S("X1_ready"), 1)
            dve.wait_ge(S("X1_ready"), 1)
            level(1).then_inc(S("M_ready"), 1)
            dve.wait_ge(S("pairs_ps"), 2)
            for t in range(TT):
                last = TTn(attn_t[:, t], bank(3 + t).rearrange("p (h n) -> p h n", h=H), dec_a[:, t], ALU.mult)
            last.then_inc(S("attn_ready"), 1)
            TTn(qn, qn, exg, ALU.mult).then_inc(S("qd_ready"), 1)
            take_mod_rows(1, 5)
            take_mod(1, 6)
            dve.wait_ge(S("U1_ps"), 1)
            CP(Um[:, 0], bank(2).rearrange("p (h n) -> p h n", h=H))
            CP(Um[:, 1], bank(7).rearrange("p (h n) -> p h n", h=H)).then_inc(S("U_ready"), 1)
            for s in range(1, LEVELS):
                dve.wait_ge(S("XMX_ps"), s)
                if s < LEVELS - 1:
                    TTn(Xm, Xm, ps[:, 3:5, :].rearrange("p t (h n) -> p t h n", h=H), ALU.subtract)
                TTn(Um, Um, ps[:, 5:7, :].rearrange("p t (h n) -> p t h n", h=H), ALU.subtract).then_inc(
                    S("U_ready"), 1)
                dve.wait_ge(S("U_ready"), s + 1)
                if s < LEVELS - 1:
                    level(s + 1).then_inc(S("M_ready"), 1)
            dve.wait_ge(S("M_ready"), LEVELS - 1)
            dve.memset(state, 0.0).then_inc(S("state_ready"), 1)
            dve.wait_ge(S("fox_ps"), 1)
            STT(fox_p0, bank(5).rearrange("p (h n) -> p h n", h=H), SCALE, fox_e0, ALU.mult, ALU.subtract)
            for j, b in enumerate((6, 0)):
                last = STT(fox_p1[:, 2 * j:2 * j + 2, :], bank(b).rearrange("p (h n) -> p h n", h=2), SCALE,
                           fox_e1[:, 2 * j:2 * j + 2, :], ALU.mult, ALU.subtract)
            last.then_inc(S("fox_s_taken"), 1)
            dve.wait_ge(S("fox_s_taken"), 1)
            dve.tensor_reduce(fmax[:, 0, :], fox_p0, AX.X, ALU.max)
            link(dve.tensor_reduce(fmax[:, 1, :], fox_p1, AX.X, ALU.max))
            TS(fmax, fmax, -1.0, None, ALU.mult).then_inc(S("fox_max_ready"), 2)
            dve.wait_ge(S("uw_taken"), 1)
            for n in range(NCH):
                t, r = n // 2, (n % 2) * CH
                rows = slice(r, r + CH)
                dve.wait_ge(S("ws_ps"), n + 1)
                TTn(vnew[rows, t], u_sb[rows, t], ps[rows, 2, :].rearrange("p (h n) -> p h n", h=H),
                    ALU.subtract).then_inc(S("vnew_ready"), 1)
                if n < NCH - 1:
                    dve.wait_ge(S("ds_ps"), n + 1)
                    for h in range(H):
                        last = STT(state[:, h, :], state[:, h, :], eg[:, h, n:n + 1], bank(7, h * P, P),
                                   ALU.mult, ALU.add)
                    last.then_inc(S("state_ready"), 1)
                    dve.wait_ge(S("state_ready"), n + 2)
                if n == 0:
                    dve.wait_ge(S("fox_exp"), 2)
                    link(dve.reciprocal(fsum, fsum))
                    TTn(fox_p0, fox_p0, fsum[:, 0, :].unsqueeze(2).to_broadcast([P, H, P]), ALU.mult)
                    TTn(fox_p1, fox_p1, fsum[:, 1, :].unsqueeze(2).to_broadcast([P, H, T]), ALU.mult).then_inc(
                        S("fox_p_ready"), 1)
            dve.wait_ge(S("oss_ready"), 1)
            for t in range(TT):
                last = per_head(o_sb[:, t], 3 + t, oss[:, t, :])
            last.then_inc(S("on_ready"), 1)
            dve.wait_ge(S("oT_ps"), 1)
            for j, b in enumerate((2, 7)):
                last = STT(oaT[:, 2 * j:2 * j + 2, :], bank(b).rearrange("p (h n) -> p h n", h=2), vec("go"),
                           zT[:, 2 * j:2 * j + 2, :], ALU.mult, ALU.mult)
            last.then_inc(S("oaT_ready"), 1)
            take_mod_rows(2, 6)
            take_mod(2, 0)
            link(STT(A2, mod[:, 32:40], 1.0, vec("g2", 0, KD), ALU.add, ALU.mult))
            dve.wait_ge(S("obT_ready"), 1)
            CP(gt2b, mod[:, 40:48].unsqueeze(2).to_broadcast([P, KD, P])).then_inc(S("gt2b_ready"), 1)
            for g in range(4):
                ba, bb = ((1, 2), (3, 4))[g % 2]
                ms = slice(2 * g, 2 * g + 2)
                dve.wait_ge(S("y_ps"), 2 * g + 1)
                TTn(merged[:, ms, :], bank(ba).rearrange("p (m n) -> p m n", m=2), gates[:, ms, :],
                    ALU.mult).then_inc(S("y_taken"), 1)
                dve.wait_ge(S("y_ps"), 2 * g + 2)
                gb_ms = gates[:, 8 + 2 * g:10 + 2 * g, :]
                ins = TTn(gb_ms, bank(bb).rearrange("p (m n) -> p m n", m=2), gb_ms, ALU.mult)
                ins.then_inc(S("y_taken"), 1)
                dve.wait_ge(S("y_taken"), 2 * g + 2)
                TTn(merged[:, ms, :], merged[:, ms, :], gb_ms, ALU.add).then_inc(S("merged_ready"), 1)
            for g in range(4):
                dve.wait_ge(S("out_ps"), g + 1)
                for m in (2 * g, 2 * g + 1):
                    last = STT(xT[:, m, :], bank((5, 6, 7, 4)[g], (m % 2) * T, T), mod[:, 16 + m:17 + m],
                               xT[:, m, :], ALU.mult, ALU.add)
                last.then_inc(S("x1_ready"), 1)
            dve.wait_ge(S("x1_ready"), 4)
            dve.wait_ge(S("rstd_ready"), 2)
            for half in range(2):
                ks = slice(4 * half, 4 * half + 4)
                ins = TTn(merged[:, ks, :], xT[:, ks, :], rs2.unsqueeze(1).to_broadcast([P, 4, T]), ALU.mult)
                ins.then_inc(S("h2_scaled"), 1)
            dve.wait_ge(S("h2_scaled"), 2)
            for k in range(4, KD):
                last = TS(merged[:, k, :], merged[:, k, :], A2[:, k:k + 1], mod[:, 24 + k:25 + k], ALU.mult, ALU.add)
            last.then_inc(S("h2T_high"), 1)
            dve.wait_ge(S("logits_ps"), 2)
            link(TTn(lg, bank(5, 256, 64).rearrange("p (t e) -> p t e", t=TT),
                     brout.unsqueeze(1).to_broadcast([P, TT, E]), ALU.add))
            for t in range(TT):
                link(dve.max(top8[:, t, :], lg[:, t, :]))
                link(dve.max_index(idx_u[:, t, :], top8[:, t, :], lg[:, t, :]))
            CP(idx8, idx_u)
            TS(ssum[:, 0:2], top8[:, :, 0], -1.0, None, ALU.mult).then_inc(S("top_ready"), 1)
            link(dve.memset(chosen, 0.0))
            for j in range(TOPK):
                for t in range(TT):
                    last = STT(chosen[:, t, :], km("iota_expert"), idx8[:, t, j:j + 1], chosen[:, t, :],
                               ALU.is_equal, ALU.add)
                if j < TOPK - 1:
                    link(last)
            last.then_inc(S("chosen_ready"), 1)
            dve.wait_ge(S("chosen_ready"), 1)
            dve.memset(gate_w, 0.0)
            dve.memset(scat, 0.0)
            dve.wait_ge(S("route_ps"), 1)
            link(STT(posm, bank(4, 0, 64).rearrange("p (t e) -> p t e", t=TT), 1.0, chosen, ALU.add, ALU.mult))
            link(TS(posm, posm, -1.0, None, ALU.add))
            CP(counts, bank(4, 64, E)).then_inc(S("slots_taken"), 1)

            def weigh_choices():
                dve.wait_ge(S("top_exp"), 1)
                link(dve.reciprocal(ssum[:, 2:4], ssum[:, 2:4]))
                link(TTn(top8[:, :, 0:TOPK], top8[:, :, 0:TOPK], ssum[:, 2:4].unsqueeze(2).to_broadcast([P, TT, TOPK]),
                         ALU.mult))
                for j in range(TOPK):
                    for t in range(TT):
                        last = TS(part[:, t, :], km("iota_expert"), idx8[:, t, j:j + 1], top8[:, t, j:j + 1],
                                  ALU.is_equal, ALU.mult)
                    link(last)
                    ins = TTn(gate_w, gate_w, part, ALU.add)
                    if j == TOPK - 1:
                        ins.then_inc(S("gate_w_ready"), 1)
                        dve.wait_ge(S("gate_w_ready"), 1)
                    else:
                        link(ins)
                dve.wait_ge(S("slots_taken"), 1)
                link(dve.tensor_reduce(rounds_part, counts, AX.X, ALU.max))
                link(TS(rounds_f, rounds_part, SLOTS + 0.5, None, ALU.is_ge))
                for n in range(2, T // SLOTS):
                    link(STT(rounds_f, rounds_part, n * SLOTS + 0.5, rounds_f, ALU.is_ge, ALU.add))
                CP(rounds_u, rounds_f).then_inc(S("rounds_ready"), 1)
                dve.wait_ge(S("route_ps"), 2)
                CP(scat[0:E, :], ps[0:E, 7, 0:T]).then_inc(S("gates_t_ready"), 1)
                dve.wait_ge(S("gt2_taken"), 1)
                dve.wait_ge(S("bdown_in"), 16)
                TTn(ypair, ypair, gt2_row, ALU.mult).then_inc(S("bdown_ready"), 1)

            def build(dst, i, weigh):
                for par in range(2):
                    for t in range(TT):
                        col = i * 2 + par
                        d = dst[:, t, par * SLOTS:(par + 1) * SLOTS]
                        if weigh:
                            last = TS(d, km("iota_slot"), posm[:, t, bass.ds(col, 1)], gate_w[:, t, bass.ds(col, 1)],
                                      ALU.is_equal, ALU.mult)
                        else:
                            last = TS(d, km("iota_slot"), posm[:, t, bass.ds(col, 1)], None, ALU.is_equal)
                return last

            def select(e, par):
                rows = ident.rearrange("p (q e) -> p q e", q=4)[:, :, bass.ds(e, 1)]
                return CP(sel[:, par], rows.to_broadcast([P, 4, SLOTS]))

            def take_xg(n):
                dve.wait_ge(S("xg_ps"), n)
                CP(xg[:, 4:8, :], bank(6).rearrange("p (k n) -> p k n", k=4)).then_inc(S("xg_ready"), 1)

            def expert(I, i, par, more):
                e = I * 2 + par
                dve.wait_ge(S("gu_used"), e * 8 + 8)
                wait_past_first(dve, S("act_t_ps"), e)
                TS(gate_a, bank(4), LIMIT, None, ALU.min).then_inc(S("gate_ready"), 1)
                TS(up_a, bank(5), LIMIT, -LIMIT, ALU.min, ALU.max).then_inc(S("up_ready"), 1)
                dve.wait_ge(S("gate_ready"), e + 1)
                dve.wait_ge(S("up_ready"), e + 1)
                STT(up_a, up_a, 1.0, gate_a, ALU.add, ALU.mult).then_inc(S("up_done"), 1)
                dve.wait_ge(S("up_done"), e + 1)
                dve.wait_ge(S("sig_ready"), e + 1)
                TTn(gate_a, up_a, sig_a, ALU.mult).then_inc(S("act_ready"), 1)
                if more:
                    select(i * 2 + (par + 2), par).then_inc(S("sel_ready"), 1)
                if par == 1 and more:
                    take_xg(I * 2 + 4)
                if par == 0 and more:
                    dve.wait_ge(S("xg_ps"), I * 2 + 2)
                    build(onehot, i + 1, False).then_inc(S("onehot_ready"), 1)
                dve.wait_ge(S("dn_used"), e * 4 + 4)
                if par == 0:
                    wait_past_first(dve, S("scattered"), I)
                for d in range(2):
                    TTn(ypair[par * 64:par * 64 + 64, d * 512:(d + 1) * 512], ps[64 * d:64 * d + 64, 6, :],
                        gt2_row[64 * d:64 * d + 64, d * 512:(d + 1) * 512], ALU.mult).then_inc(S("y_moved"), 1)
                if par == 0:
                    dve.wait_ge(S("scat_ps"), I + 1)
                    CP(scat, bank(7, 0, T)).then_inc(S("scat_ready"), 1)
                    if more:
                        build(gated, i + 1, True).then_inc(S("gated_ready"), 1)

            def one_round(q):
                first = isinstance(q, int)
                I0 = q * PAIRS
                build(onehot, 0, False).then_inc(S("onehot_ready"), 1)
                if first:
                    dve.wait_ge(S("h2tok_ps"), 2)
                for par in range(2):
                    select(par, par).then_inc(S("sel_ready"), 1)
                take_xg(I0 * 2 + 2)
                if first:
                    weigh_choices()
                build(gated, 0, True).then_inc(S("gated_ready"), 1)
                for par in range(2):
                    expert(I0, 0, par, True)
                with dve.Fori(1, PAIRS - 1) as i:
                    for par in range(2):
                        expert(I0 + i, i, par, True)
                for par in range(2):
                    expert(I0 + (PAIRS - 1), PAIRS - 1, par, False)

            def later_round(q):
                dve.wait_ge(S("scattered"), q * PAIRS)
                TS(posm, posm, -float(SLOTS), None, ALU.add).then_inc(S("posm_moved"), 1)
                dve.wait_ge(S("posm_moved"), q)
                one_round(q)

            one_round(0)
            extra_rounds(dve, later_round)
            dve.wait_ge(S("gfin_in"), 16)
            for t in range(TT):
                dve.wait_ge(S("root_ready"), t + 1)
                link(dve.reciprocal(oss[:, 1, t:t + 1], oss[:, 1, t:t + 1]))
                STT(x2[:, t, :].rearrange("p (b n) -> p b n", b=2), ps[:, 2 * t:2 * t + 2, :], oss[:, 1, t:t + 1],
                    flat[:, 0:1024].rearrange("p (b n) -> p b n", b=2), ALU.mult, ALU.mult).then_inc(S("out_sb"), 1)

        @block.gpsimd
        def _(pool):
            pool.memset(raw[:, :, 0:3], 0.0).then_inc(S("zeroed"), 1)
            pool.wait_ge(S("h2_scaled"), 2)
            pool.wait_ge(S("x1_summed"), 1)
            pool.memset(ypair, 0.0).then_inc(S("zeroed"), 1)
            pool.wait_ge(S("zeroed"), 2)
            pool.dma_start(ypair[0:E, :], b_down[0]).then_inc(S("bdown_in"), 16)
            pool.wait_ge(S("h2tok_ps"), TT)
            for q in range(4):
                pool.dma_start(bias_gu[E * q:E * q + E, :], b_gate_up[0, :, 512 * q:512 * q + 512]).then_inc(
                    S("bias_in"), 16)



_INS = ["x", "c", "w_ada", "b_ada", "g_norm1", "w_in", "conv_w", "a_log", "dt_bias", "g_onorm", "b_fgate",
        "w_o_delta", "w_o_fox", "w_out", "g_norm2", "w_router", "b_router", "w_gate_up", "b_gate_up",
        "w_down", "b_down", "g_final"]


def constant_masks():
    import numpy as np

    r = np.arange(P)[:, None]
    q = np.arange(P)[None, :]
    same = (r // 64) == (q // 64)
    m = {"ident": r == q, "iota_slot": np.broadcast_to(np.arange(64), (P, 64)),
         "iota_expert": np.broadcast_to(np.arange(32), (P, 32)), "rms_eps": np.full((P, 1), 1e-6),
         "cum_chunk": same & (r <= q), "suffix_chunk": same & (r > q), "cum_all_ones": np.concatenate([r <= q, np.ones((P, P))], 1), "ones": np.ones((P, P)),
         "before": r < q,
         "outside_strict": np.where(same & (q < r), 0.0, BIG), "outside_incl_t": np.where(same & (q >= r), 0.0, BIG),
         "fox_open": np.zeros((P, P)), "fox_outside": np.where(q <= r, 0.0, BIG)}
    for s in range(6):
        w = 2 << s
        m[f"level{s}"] = (r // w == q // w) & (r % w >= w // 2) & (q % w < w // 2)
    packs = []
    for d, n in mask_columns():
        a = np.zeros((P, n), np.float32)
        for name, (at, w) in d.items():
            a[:, at:at + w] = m[name]
        packs.append(a)
    return packs


def kernel(**inputs):
    import numpy as _np
    import concourse.bacc as _bacc
    from concourse import mybir as _mybir
    from concourse.bass_utils import run_bass_kernel_spmd as _run

    nc = _bacc.Bacc("TRN2", target_bir_lowering=False, num_devices=1)
    arrays, args = {}, []
    values = [(n, inputs[n]) for n in _INS]
    values += list(zip(("kept_masks", "early_masks"), constant_masks()))
    for name, value in values:
        a = _np.ascontiguousarray(value)
        arrays[f"in_{name}_dram"] = a
        args.append(nc.dram_tensor(f"in_{name}_dram", a.shape, _mybir.dt.from_np(a.dtype), kind="ExternalInput").ap())
    shape = inputs["x"].shape
    args.append(nc.dram_tensor("out_0_dram", shape, _mybir.dt.float32, kind="ExternalOutput").ap())
    layer_kernel(nc, *args)
    r = _run(nc, [arrays], core_ids=[0])
    return r.results[0]["out_0_dram"]
```
